# Optimizing a Trainium2 kernel written in Bass

```python
import jax, jax.numpy as jnp
from jax import lax
import numpy as np

D_MODEL = 1024
BATCH = 1
SEQ = 256
DEPTH = 2

CHUNK = 64
N_BRANCH = 4
W_BRANCH = 512
LRU_HEADS = 8
LRU_BLOCK = W_BRANCH // LRU_HEADS
LRU_CONV = 4
LRU_C = 8.0
SWA_HEADS = 8
SWA_KV_HEADS = 2
SWA_HEAD_DIM = W_BRANCH // SWA_HEADS
SWA_WINDOW = 128
SWA_PREV_CHUNKS = SWA_WINDOW // CHUNK - 1
ROPE_THETA = 10000.0
MLSTM_HEADS = 4
MLSTM_HEAD_DIM = W_BRANCH // MLSTM_HEADS
CONV_WIDTH = 31
D_FF = 2816
FFN_RESIDUAL = 0.5
PLE_DIM = 256
N_NORMS = 4
LN_EPS = 1e-5
DEEPNORM_ALPHA = (2 * DEPTH) ** 0.25
DEEPNORM_BETA = (8 * DEPTH) ** -0.25
MASK_VALUE = -1e30

_COLS = (W_BRANCH, W_BRANCH,
         SWA_HEADS * SWA_HEAD_DIM, SWA_KV_HEADS * SWA_HEAD_DIM, SWA_KV_HEADS * SWA_HEAD_DIM,
         W_BRANCH, W_BRANCH, W_BRANCH, W_BRANCH, MLSTM_HEADS, MLSTM_HEADS,
         W_BRANCH, W_BRANCH,
         N_BRANCH * D_MODEL)
SPLIT_POINTS = tuple(int(c) for c in np.cumsum(_COLS)[:-1])
N_IN = int(sum(_COLS))
MLSTM_F_COL = SPLIT_POINTS[9]

kernel_name = 'hybrid_gated_streaming_encoder'

def _layernorm(x, g, b):
    xf = x.astype(jnp.float32)
    mu = jnp.mean(xf, axis=-1, keepdims=True)
    var = jnp.mean(jnp.square(xf - mu), axis=-1, keepdims=True)
    return ((xf - mu) * lax.rsqrt(var + LN_EPS) * g + b).astype(x.dtype)

def _swiglu(x, w_in, w_out):
    gate, up = jnp.split(x @ w_in, 2, axis=-1)
    return (jax.nn.silu(gate) * up) @ w_out

def _causal_dwconv(x, w, b):
    K, C = w.shape
    out = lax.conv_general_dilated(
        x, w[:, None, :].astype(x.dtype), window_strides=(1,), padding=[(K - 1, 0)],
        dimension_numbers=('NWC', 'WIO', 'NWC'), feature_group_count=C)
    return out + b

def _rglru(x, w_rg, b_rg, lam):
    B, S, W = x.shape
    xb = x.reshape(B, S, LRU_HEADS, LRU_BLOCK)
    gates = jnp.einsum('bshi,ghij->gbshj', xb, w_rg).reshape(2, B, S, W) + b_rg[:, None, None, :]
    r = jax.nn.sigmoid(gates[0].astype(jnp.float32))
    i = jax.nn.sigmoid(gates[1].astype(jnp.float32))
    log_a = -LRU_C * r * jax.nn.softplus(-lam.astype(jnp.float32))
    a = jnp.exp(log_a)
    u = jnp.sqrt(-jnp.expm1(2.0 * log_a)) * (i * x.astype(jnp.float32))

    def combine(left, right):
        a_l, b_l = left
        a_r, b_r = right
        return a_l * a_r, a_r * b_l + b_r

    _, h = lax.associative_scan(combine, (a, u), axis=1)
    return h.astype(x.dtype)

def _rope(t, pos):
    half = t.shape[-1] // 2
    inv = ROPE_THETA ** (-jnp.arange(half, dtype=jnp.float32) / half)
    ang = pos.astype(jnp.float32)[:, None] * inv[None, :]
    cos = jnp.cos(ang)[None, :, None, :]
    sin = jnp.sin(ang)[None, :, None, :]
    tf = t.astype(jnp.float32)
    t1, t2 = tf[..., :half], tf[..., half:]
    return jnp.concatenate([t1 * cos - t2 * sin, t2 * cos + t1 * sin], axis=-1).astype(t.dtype)

def _chunk_band(t, n_prev):
    nC = t.shape[1]
    pad = jnp.pad(t, [(0, 0), (n_prev, 0)] + [(0, 0)] * (t.ndim - 2))
    return jnp.concatenate([pad[:, j:j + nC] for j in range(n_prev + 1)], axis=2)

def _swa_sink_attention(q, k, v, sinks):
    B, S, H, dh = q.shape
    nC = S // CHUNK
    G = H // SWA_KV_HEADS
    pos = jnp.arange(S, dtype=jnp.int32)
    q = _rope(q, pos)
    k = _rope(k, pos)
    qc = q.reshape(B, nC, CHUNK, SWA_KV_HEADS, G, dh)
    kc = _chunk_band(k.reshape(B, nC, CHUNK, SWA_KV_HEADS, dh), SWA_PREV_CHUNKS)
    vc = _chunk_band(v.reshape(B, nC, CHUNK, SWA_KV_HEADS, dh), SWA_PREV_CHUNKS)
    Wk = (SWA_PREV_CHUNKS + 1) * CHUNK
    scores = jnp.einsum('bcqkgd,bcjkd->bkgcqj', qc, kc,
                        preferred_element_type=jnp.float32) * (dh ** -0.5)
    key_chunk = jnp.arange(nC)[:, None] - SWA_PREV_CHUNKS + (jnp.arange(Wk) // CHUNK)[None, :]
    valid = key_chunk >= 0
    scores = jnp.where(valid[:, None, :], scores, MASK_VALUE)
    sink = jnp.broadcast_to(sinks.astype(jnp.float32).reshape(1, SWA_KV_HEADS, G, 1, 1, 1),
                            scores.shape[:-1] + (1,))
    probs = jax.nn.softmax(jnp.concatenate([scores, sink], axis=-1), axis=-1)[..., :-1]
    out = jnp.einsum('bkgcqj,bcjkd->bcqkgd', probs.astype(v.dtype), vc)
    return out.reshape(B, S, H * dh)

def _mlstm(q, k, v, i_pre, f_pre):
    B, S, H, d = q.shape
    nC = S // CHUNK
    L = CHUNK
    f32 = jnp.float32

    def heads(t):
        return t.astype(f32).reshape(B, nC, L, H, -1).transpose(0, 3, 1, 2, 4)

    qh = heads(q)
    kh = heads(k) * (d ** -0.5)
    vh = heads(v)
    ig = i_pre.astype(f32).reshape(B, nC, L, H).transpose(0, 3, 1, 2)
    lf = jax.nn.log_sigmoid(f_pre.astype(f32)).reshape(B, nC, L, H).transpose(0, 3, 1, 2)
    bcum = jnp.cumsum(lf, axis=-1)
    g = bcum[..., -1]
    a = g[..., None] - bcum + ig
    m_loc = jnp.max(a, axis=-1)
    w = jnp.exp(a - m_loc[..., None])
    kv = jnp.einsum('bhcl,bhcle,bhcld->bhced', w, vh, kh)
    ksum = jnp.einsum('bhcl,bhcld->bhcd', w, kh)

    def step(carry, inp):
        C, n, m = carry
        kv_c, ks_c, g_c, ml_c = inp
        m_new = jnp.maximum(g_c + m, ml_c)
        s_old = jnp.exp(g_c + m - m_new)
        s_new = jnp.exp(ml_c - m_new)
        C_new = s_old[..., None, None] * C + s_new[..., None, None] * kv_c
        n_new = s_old[..., None] * n + s_new[..., None] * ks_c
        return (C_new, n_new, m_new), (C, n, m)

    init = (jnp.zeros((B, H, d, d), f32), jnp.zeros((B, H, d), f32), jnp.zeros((B, H), f32))
    xs = (kv.transpose(2, 0, 1, 3, 4), ksum.transpose(2, 0, 1, 3),
          g.transpose(2, 0, 1), m_loc.transpose(2, 0, 1))
    _, (C_prev, n_prev, m_prev) = lax.scan(step, init, xs)
    C_prev = C_prev.transpose(1, 2, 0, 3, 4)
    n_prev = n_prev.transpose(1, 2, 0, 3)
    m_prev = m_prev.transpose(1, 2, 0)
    causal = jnp.tril(jnp.ones((L, L), dtype=bool))
    Dlog = jnp.where(causal, bcum[..., :, None] - bcum[..., None, :] + ig[..., None, :], -jnp.inf)
    inter_log = bcum + m_prev[..., None]
    m_t = jnp.maximum(jnp.max(Dlog, axis=-1), inter_log)
    sc = jnp.exp(Dlog - m_t[..., None]) * jnp.einsum('bhctd,bhcsd->bhcts', qh, kh)
    inter_w = jnp.exp(inter_log - m_t)
    num = (jnp.einsum('bhcts,bhcse->bhcte', sc, vh)
           + inter_w[..., None] * jnp.einsum('bhctd,bhced->bhcte', qh, C_prev))
    den = jnp.sum(sc, axis=-1) + inter_w * jnp.einsum('bhctd,bhcd->bhct', qh, n_prev)
    h = num / jnp.maximum(jnp.abs(den), jnp.exp(-m_t))[..., None]
    return h.transpose(0, 2, 3, 1, 4).reshape(B, S, H * d).astype(q.dtype)

def _token_mix(x, w_in, b_in, conv_w, conv_b, w_rg, b_rg, lru_lambda, sinks,
               dw_w, dw_b, cln_g, cln_b, w_br, w_out):
    B, S, _ = x.shape
    proj = x @ w_in + b_in
    (a_x, a_y, b_q, b_k, b_v, c_q, c_k, c_v, c_o, c_i, c_f,
     d_a, d_g, gates) = jnp.split(proj, SPLIT_POINTS, axis=-1)
    u = _causal_dwconv(a_x, conv_w, conv_b)
    h_a = _rglru(u, w_rg, b_rg, lru_lambda) * jax.nn.gelu(a_y)
    h_b = _swa_sink_attention(b_q.reshape(B, S, SWA_HEADS, SWA_HEAD_DIM),
                              b_k.reshape(B, S, SWA_KV_HEADS, SWA_HEAD_DIM),
                              b_v.reshape(B, S, SWA_KV_HEADS, SWA_HEAD_DIM), sinks)
    h_c = _mlstm(c_q.reshape(B, S, MLSTM_HEADS, MLSTM_HEAD_DIM),
                 c_k.reshape(B, S, MLSTM_HEADS, MLSTM_HEAD_DIM),
                 c_v.reshape(B, S, MLSTM_HEADS, MLSTM_HEAD_DIM), c_i, c_f) * jax.nn.sigmoid(c_o)
    glu = d_a * jax.nn.sigmoid(d_g)
    h_d = jax.nn.silu(_layernorm(_causal_dwconv(glu, dw_w, dw_b), cln_g, cln_b))
    gate = jax.nn.sigmoid(gates.reshape(B, S, N_BRANCH, D_MODEL))
    branches = (h_a, h_b, h_c, h_d)
    merged = gate[:, :, 0] * (branches[0] @ w_br[0])
    for n in range(1, N_BRANCH):
        merged = merged + gate[:, :, n] * (branches[n] @ w_br[n])
    return merged @ w_out

def setup_inputs(seed: int = 0) -> dict:
    key = jax.random.key(seed)
    ks = jax.random.split(key, 24)
    f32 = jnp.float32

    def nrm(k, shape, fan_in, scale=1.0):
        return jax.random.normal(k, shape, f32) * (scale * fan_in ** -0.5)

    def small(k, shape, s=0.02):
        return jax.random.normal(k, shape, f32) * s

    x = jax.random.normal(ks[0], (BATCH, SEQ, D_MODEL), f32)
    p = jax.random.normal(ks[1], (DEPTH, BATCH, SEQ, PLE_DIM), f32)
    ln_g = 1.0 + small(ks[2], (DEPTH, N_NORMS, D_MODEL))
    ln_b = small(ks[3], (DEPTH, N_NORMS, D_MODEL))
    ffn_w_in = nrm(ks[4], (DEPTH, 2, D_MODEL, 2 * D_FF), D_MODEL)
    ffn_w_out = nrm(ks[5], (DEPTH, 2, D_FF, D_MODEL), D_FF, DEEPNORM_BETA)
    w_in = nrm(ks[6], (DEPTH, D_MODEL, N_IN), D_MODEL)
    b_in = small(ks[7], (DEPTH, N_IN))
    b_in = b_in.at[:, MLSTM_F_COL:MLSTM_F_COL + MLSTM_HEADS].add(
        jnp.linspace(3.0, 6.0, MLSTM_HEADS, dtype=f32))
    conv_w = nrm(ks[8], (DEPTH, LRU_CONV, W_BRANCH), LRU_CONV)
    conv_b = small(ks[9], (DEPTH, W_BRANCH))
    w_rg = nrm(ks[10], (DEPTH, 2, LRU_HEADS, LRU_BLOCK, LRU_BLOCK), LRU_BLOCK)
    b_rg = small(ks[11], (DEPTH, 2, W_BRANCH))
    a_c = jax.random.uniform(ks[12], (DEPTH, W_BRANCH), f32, 0.9, 0.999)
    a_base = a_c ** (1.0 / LRU_C)
    lru_lambda = jnp.log(a_base) - jnp.log1p(-a_base)
    sinks = small(ks[13], (DEPTH, SWA_HEADS), 0.5)
    dw_w = nrm(ks[14], (DEPTH, CONV_WIDTH, W_BRANCH), CONV_WIDTH)
    dw_b = small(ks[15], (DEPTH, W_BRANCH))
    cln_g = 1.0 + small(ks[16], (DEPTH, W_BRANCH))
    cln_b = small(ks[17], (DEPTH, W_BRANCH))
    w_br = nrm(ks[18], (DEPTH, N_BRANCH, W_BRANCH, D_MODEL), W_BRANCH, DEEPNORM_BETA)
    w_out = nrm(ks[19], (DEPTH, D_MODEL, D_MODEL), D_MODEL, DEEPNORM_BETA)
    ple_w = nrm(ks[20], (DEPTH, PLE_DIM, D_MODEL), PLE_DIM, DEEPNORM_BETA)
    ple_gate_w = nrm(ks[21], (DEPTH, D_MODEL, D_MODEL), D_MODEL)
    ple_gate_b = small(ks[22], (DEPTH, D_MODEL))
    return {'x': x, 'p': p, 'ln_g': ln_g, 'ln_b': ln_b,
            'ffn_w_in': ffn_w_in, 'ffn_w_out': ffn_w_out,
            'w_in': w_in, 'b_in': b_in, 'conv_w': conv_w, 'conv_b': conv_b,
            'w_rg': w_rg, 'b_rg': b_rg, 'lru_lambda': lru_lambda, 'sinks': sinks,
            'dw_w': dw_w, 'dw_b': dw_b, 'cln_g': cln_g, 'cln_b': cln_b,
            'w_br': w_br, 'w_out': w_out,
            'ple_w': ple_w, 'ple_gate_w': ple_gate_w, 'ple_gate_b': ple_gate_b}

def reference(x, p, ln_g, ln_b, ffn_w_in, ffn_w_out, w_in, b_in, conv_w, conv_b,
              w_rg, b_rg, lru_lambda, sinks, dw_w, dw_b, cln_g, cln_b, w_br, w_out,
              ple_w, ple_gate_w, ple_gate_b):
    for i in range(DEPTH):
        x = _layernorm(DEEPNORM_ALPHA * x + FFN_RESIDUAL * _swiglu(x, ffn_w_in[i, 0], ffn_w_out[i, 0]),
                       ln_g[i, 0], ln_b[i, 0])
        mix = _token_mix(x, w_in[i], b_in[i], conv_w[i], conv_b[i], w_rg[i], b_rg[i],
                         lru_lambda[i], sinks[i], dw_w[i], dw_b[i], cln_g[i], cln_b[i],
                         w_br[i], w_out[i])
        x = _layernorm(DEEPNORM_ALPHA * x + mix, ln_g[i, 1], ln_b[i, 1])
        x = _layernorm(DEEPNORM_ALPHA * x + FFN_RESIDUAL * _swiglu(x, ffn_w_in[i, 1], ffn_w_out[i, 1]),
                       ln_g[i, 2], ln_b[i, 2])
        e = jax.nn.sigmoid(x @ ple_gate_w[i] + ple_gate_b[i]) * (p[i] @ ple_w[i])
        x = _layernorm(DEEPNORM_ALPHA * x + e, ln_g[i, 3], ln_b[i, 3])
    return x


_drawn_inputs = setup_inputs


def setup_inputs(seed=0):
    import zlib

    import numpy as np

    out = dict(_drawn_inputs(seed))
    spreads = {}
    factors = {'conv_b': 4.732,
     'b_rg': 64.0,
     'sinks': 27.491,
     'dw_b': 5.074,
     'cln_g': 8.0,
     'cln_b': 8.0,
     'ple_gate_b': 8.0}
    for name, (base, spread) in spreads.items():
        noise = np.random.default_rng([zlib.crc32(name.encode()), seed]).standard_normal(out[name].shape)
        drawn = base * np.exp(spread * noise) if base else spread * noise
        out[name] = __import__('jax').numpy.asarray(drawn.astype(out[name].dtype))
    for name, factor in factors.items():
        out[name] = (out[name] * factor).astype(out[name].dtype)
    return out
```

```python
from contextlib import ExitStack

import numpy as np

import concourse.bass as bass
from concourse import mybir

F32 = mybir.dt.float32
F32R = mybir.dt.float32r
ALU = mybir.AluOpType
ACT = mybir.ActivationFunctionType
AX_X = mybir.AxisListType.X

P = 128
DEPTH = 2
T = 256
TT = T // P
D = 1024
KD = D // P
DFF = 2816
NFF = DFF // 256
W = 512
KW = W // P
NB = 4
L = 64
NCH = T // L
PAD = L
TAPS = 31
LTAPS = 4
HEADS_C = 4
ALPHA = float((2 * DEPTH) ** 0.25)
EPS = 1e-5
MASKED = -1e30
RING = 3
SLOT = 2048

A_X, A_Y, B_Q, B_K, B_V = 0, 512, 1024, 1536, 1664
C_Q, C_K, C_V, C_O, C_I, C_F = 1792, 2304, 2816, 3328, 3840, 3844
D_A, D_G, GATES = 3848, 4360, 4872
N_IN = 8968
GROUPS = [D_G, D_A, A_X, A_Y, C_Q, C_K, C_V, C_O, B_Q, "kv"]
ORDER = [0, 2, 3, 1]

FFN_CHUNKS = 3 * NFF
AT_FFN1 = 0
AT_IN = AT_FFN1 + FFN_CHUNKS
AT_STEP = AT_IN + 2 * len(GROUPS)
AT_OUT = AT_STEP + 3 * 2 * NB
AT_FFN2 = AT_OUT + 4
AT_PG = AT_FFN2 + FFN_CHUNKS
AT_PW = AT_PG + 4
CHUNKS = AT_PW + 1

PC_IN = 0
PC_K2 = 70
PC_CW, PC_CB, PC_RG, PC_LAM = 72, 88, 92, 100
PC_DB, PC_CG, PC_CLB = 104, 108, 112
ROWS0 = 116
PC_DW = 116
PC_G = PC_DW + TAPS * KW
PC_B = PC_G + 32
PCN = PC_B + 32

K_ID, K_TRI, K_ROT, K_COS, K_SIN, K_SEL, K_ONE = 0, 128, 256, 384, 640, 896, 1408
K_N = K_ONE + 256


def bias_col(off):
    return PC_IN + (off // P if off < C_I else 30 + (off - D_A) // P)


def constants():
    c = np.zeros((P, K_N), np.float32)
    i = np.arange(P)
    c[i, K_ID + i] = 1.0
    c[:, K_TRI:K_TRI + P] = i[None, :] >= i[:, None]
    for m in range(P):
        if m % 64 < 32:
            c[m + 32, K_ROT + m] = -1.0
        else:
            c[m - 32, K_ROT + m] = 1.0
    inv = np.float32(10000.0) ** (-np.arange(32, dtype=np.float32) / np.float32(32))
    ang = np.arange(T, dtype=np.float32)[None, :] * inv.astype(np.float32)[i % 32][:, None]
    c[:, K_COS:K_COS + T] = np.cos(ang)
    c[:, K_SIN:K_SIN + T] = np.sin(ang)
    for h in range(HEADS_C):
        c[h, K_SEL + P * h:K_SEL + P * (h + 1)] = 1.0
    c[:, K_ONE:] = 1.0
    return c


def build(nc, x, p, ln_g, ln_b, ffn_w_in, ffn_w_out, w_in, b_in, conv_w, conv_b, w_rg, b_rg,
          lru_lambda, sinks, dw_w, dw_b, cln_g, cln_b, w_br, w_out, ple_w, ple_gate_w, ple_gate_b,
          consts, out):
    ctx = ExitStack()
    with ctx:
        def sb(name, shape, dt=F32):
            return ctx.enter_context(nc.sbuf_tensor(name, shape, dt))

        def sem(name):
            return ctx.enter_context(nc.semaphore(name))

        raw = sb("raw", [P, RING, SLOT])
        whi = sb("whi", [P, RING, SLOT], F32R)
        wlo = sb("wlo", [P, RING, SLOT], F32R)
        xtok = sb("xtok", [P, TT, D])
        big = sb("big", [P, 2176])
        r = big[:, 0:TT * D].rearrange("p (t d) -> p t d", t=TT)
        g_bc = sb("g_bc", [P, D])
        b_bc = sb("b_bc", [P, D])
        wide = sb("wide", [P, 2080])
        xT = wide[:, 0:KD * T].rearrange("p (k t) -> p k t", k=KD)
        xhi = sb("xhi", [P, KD, PAD + T], F32R)
        xlo = sb("xlo", [P, KD, PAD + T], F32R)
        hhi = sb("hhi", [P, 2, 2, T], F32R)
        hlo = sb("hlo", [P, 2, 2, T], F32R)
        bhi = sb("bhi", [P, 2, KW, T], F32R)
        blo = sb("blo", [P, 2, KW, T], F32R)
        S = sb("S", [P, 8, 1024])
        kc = sb("kc", [P, K_N])
        pc = sb("pc", [P, DEPTH, PCN])
        wbd = sb("wbd", [P, 2 * KW, P])
        wif = sb("wif", [P, KD, 8])
        bif = sb("bif", [4, 2])
        cvb = sb("cvb", [P, W])
        bvb = sb("bvb", [P, P])
        snk = sb("snk", [P, 8])
        rows = sb("rows", [4, 3, T])
        vare = sb("vare", [P, TT])
        rstd = sb("rstd", [P, TT])
        stats = sb("stats", [P, TT, 2, 6])
        mv = sb("mv", [P, TT, 2])
        lam4 = sb("lam4", [P, DEPTH, KW])
        spt = sb("spt", [P, 6, 2 * KW])
        acol = sb("acol", [P, 4, 4])
        emm = sb("emm", [P, 2, 4])
        den = sb("den", [P, 3, 8])
        soft = sb("soft", [P, 5, 16])
        ones_d = sb("ones_d", [P, P])
        half = sb("half", [P, 2])

        gl = big[:, 0:KW * (T + TAPS - 1)].rearrange("p (m t) -> p m t", m=KW)
        yc = big[:, 1144:1144 + 1024].rearrange("p (m t) -> p m t", m=KW)
        axp = wide[:, 0:KW * (T + LTAPS - 1)].rearrange("p (m t) -> p m t", m=KW)
        vext = wide[:, 1040:1040 + 1032].rearrange("p (s h e) -> p s h e", s=2, h=4)
        merged = xT

        def s4(i):
            return S[:, i, :].rearrange("p (m t) -> p m t", m=KW)

        E = S[:, 2:4, :].rearrange("p a b -> p (a b)")[:, 0:1536].rearrange("p (h t) -> p h t", h=4)
        scT = S[:, 4:6, :].rearrange("p a b -> p (a b)")[:, 0:1536].rearrange("p (h t) -> p h t", h=4)
        Eflat = S[:, 2:4, :].rearrange("p a b -> p (a b)")[:, 0:1536]
        qraw = S[:, 6:8, :].rearrange("p a b -> p (a b)")[:, 0:1536].rearrange("p (m t) -> p m t", m=6)
        qrot = S[:, 4:6, :].rearrange("p a b -> p (a b)")[:, 0:1536].rearrange("p (m t) -> p m t", m=6)
        qr = S[:, 2, :].rearrange("p (m t) -> p m t", m=4)
        kr = S[:, 3, 0:2 * (PAD + T)].rearrange("p (m t) -> p m t", m=2)
        Pm = S[:, 6:8, :].rearrange("p a (h j) -> p a h j", h=8)
        PT = S[:, 4:6, :].rearrange("p a (h j) -> p a h j", h=8)
        vw = sb("vw", [P, NCH, P])
        sg = s4(0)
        sil = S[:, 0, 0:512].rearrange("p (q t) -> p q t", q=2)
        hf = S[:, 1, 0:512].rearrange("p (q t) -> p q t", q=2)

        ps = ctx.enter_context(nc.psum_tensor("ps", [P, 8, 512], F32))

        ident = kc[:, K_ID:K_ID + P]

        raw_full = [sem(f"raw_full{i}") for i in range(RING)]
        a_made = sem("a_made")
        acc0_done = sem("acc0_done")
        act_step = sem("act_step")
        ax_made = sem("ax_made")
        bA_made = sem("bA_made")
        bB_made = sem("bB_made")
        bC_made = sem("bC_made")
        bD_made = sem("bD_made")
        bhi_made = sem("bhi_made")
        bk_made = sem("bk_made")
        blo_made = sem("blo_made")
        bq_made = sem("bq_made")
        chunk_used = sem("chunk_used")
        ck_made = sem("ck_made")
        co_made = sem("co_made")
        consts_in = sem("consts_in")
        conv_tap = sem("conv_tap")
        cq_made = sem("cq_made")
        cv_made = sem("cv_made")
        d_made = sem("d_made")
        dn_made = sem("dn_made")
        dsq_made = sem("dsq_made")
        dstd_made = sem("dstd_made")
        dvar_done = sem("dvar_done")
        dvar_made = sem("dvar_made")
        e_arg = sem("e_arg")
        e_made = sem("e_made")
        emm_made = sem("emm_made")
        f_abs = sem("f_abs")
        f_exp = sem("f_exp")
        gate0_done = sem("gate0_done")
        gates_made = sem("gates_made")
        gb_in = sem("gb_in")
        gelu_made = sem("gelu_made")
        glu_made = sem("glu_made")
        h_made = sem("h_made")
        hc_T = sem("hc_T")
        hc_made = sem("hc_made")
        hhi_made = sem("hhi_made")
        hlo_made = sem("hlo_made")
        if_done = sem("if_done")
        kq_done = sem("kq_done")
        lam_abs = sem("lam_abs")
        lam_exp = sem("lam_exp")
        lam_made = sem("lam_made")
        lay_in = sem("lay_in")
        mean_done = sem("mean_done")
        mhi_made = sem("mhi_made")
        mlo_made = sem("mlo_made")
        num_done = sem("num_done")
        om_made = sem("om_made")
        om_sqrt = sem("om_sqrt")
        out_done = sem("out_done")
        pT_made = sem("pT_made")
        p_T = sem("p_T")
        p_arg = sem("p_arg")
        p_exp = sem("p_exp")
        p_in = sem("p_in")
        p_made = sem("p_made")
        p_turned = sem("p_turned")
        pads_made = sem("pads_made")
        pb_in = sem("pb_in")
        pg0_done = sem("pg0_done")
        phi_made = sem("phi_made")
        plo_made = sem("plo_made")
        pool_step = sem("pool_step")
        prod_made = sem("prod_made")
        prow_T = sem("prow_T")
        pt_made = sem("pt_made")
        pv_done = sem("pv_done")
        rg_done = sem("rg_done")
        rope_made = sem("rope_made")
        rot_done = sem("rot_done")
        rows_T = sem("rows_T")
        rows_in = [sem(f"rows_in{l}") for l in range(DEPTH)]
        rows_made = sem("rows_made")
        rstd_made = sem("rstd_made")
        s_done = sem("s_done")
        s_out = sem("s_out")
        sc_made = sem("sc_made")
        sgd_made = sem("sgd_made")
        sig_made = sem("sig_made")
        silu_made = sem("silu_made")
        u_made = sem("u_made")
        var_made = sem("var_made")
        vec_step = sem("vec_step")
        vw_made = sem("vw_made")
        whi_made = sem("whi_made")
        wlo_made = sem("wlo_made")
        xT_made = sem("xT_made")
        x_in = sem("x_in")
        xhat_T = sem("xhat_T")
        xhat_made = sem("xhat_made")
        xhi_made = sem("xhi_made")
        xlo_made = sem("xlo_made")
        xtok_made = sem("xtok_made")
        z_made = sem("z_made")
        zs_made = sem("zs_made")
        phi = bhi[:, 0, 0:2, :]
        plo = blo[:, 0, 0:2, :]

        block = ctx.enter_context(nc.Block())

        @block.sync
        def _(sp):
            def chunk(c, src, shape, j=0):
                slot = c % RING
                if not (isinstance(j, int) and c < RING):
                    sp.wait_ge(wlo_made, RING * j + (c - RING + 1))
                n = int(np.prod(shape))
                dst = raw[:, slot, 0:n]
                if len(shape) == 2:
                    dst = dst.rearrange("p (k n) -> p k n", k=shape[0])
                elif len(shape) == 3:
                    dst = dst.rearrange("p (k u n) -> p k u n", k=shape[0], u=shape[1])
                for u in range(2):
                    a = (slice(None), slice(None), u) if len(shape) == 3 else \
                        (slice(None), slice(u * shape[0] // 2, (u + 1) * shape[0] // 2))
                    sp.dma_start(dst[a], src[a]).then_inc(raw_full[slot], 16)

            def tiles(w, k0, kn, c0, cn):
                return w.rearrange("(k p) n -> p k n", p=P)[:, k0:k0 + kn, c0:c0 + cn]

            def ffn(c0, l, f):
                win = ffn_w_in[l, f].rearrange("(k p) (u n) -> p k u n", p=P, u=2)
                wout = ffn_w_out[l, f].rearrange("(k p) n -> p k n", p=P)

                def gate_up(c, j, kk, jj=0):
                    chunk(c, win[:, 4 * kk:4 * kk + 4, :, bass.ts(j, 256)], (4, 2, 256), jj)

                gate_up(c0, 0, 0)
                gate_up(c0 + 1, 0, 1)
                gate_up(c0 + 2, 1, 0)
                gate_up(c0 + 3, 1, 1)
                chunk(c0 + 4, wout[:, 0:2, :], (2, 1024))
                with sp.Fori(1, NFF - 1) as j:
                    gate_up(c0 + 2, j + 1, 0, j)
                    gate_up(c0 + 3, j + 1, 1, j)
                    chunk(c0 + 4, wout[:, bass.ts(j, 2), :], (2, 1024), j)
                chunk(c0 + 32, wout[:, 2 * (NFF - 1):2 * NFF, :], (2, 1024))

            sp.dma_start(kc[:, :], consts).then_inc(consts_in, 16)
            for l in range(DEPTH):
                base = l * CHUNKS
                ffn(base + AT_FFN1, l, 0)
                for g, off in enumerate(GROUPS):
                    for kk in range(2):
                        c = base + AT_IN + 2 * g + kk
                        if off == "kv":
                            chunk(c, tiles(w_in[l], 4 * kk, 4, B_K, 2 * P), (4, 2 * P))
                        else:
                            chunk(c, tiles(w_in[l], 4 * kk, 4, off, W), (4, W))
                c = base + AT_STEP
                for n in ORDER:
                    for hf_ in range(2):
                        for kk in range(2):
                            chunk(c, tiles(w_in[l], 4 * kk, 4, GATES + n * D + hf_ * W, W), (4, W))
                            c += 1
                        chunk(c, tiles(w_br[l, n], 0, 4, hf_ * W, W), (4, W))
                        c += 1
                for cg in range(2):
                    for kk in range(2):
                        chunk(c, tiles(w_out[l], 4 * kk, 4, cg * W, W), (4, W))
                        c += 1
                ffn(base + AT_FFN2, l, 1)
                c = base + AT_PG
                for cg in range(2):
                    for kk in range(2):
                        chunk(c, tiles(ple_gate_w[l], 4 * kk, 4, cg * W, W), (4, W))
                        c += 1
                chunk(c, tiles(ple_w[l], 0, 2, 0, D), (2, D))

        @block.gpsimd
        def _(pool):
            step = [0]

            def link(ins):
                step[0] += 1
                ins.then_inc(pool_step, 1)
                pool.wait_ge(pool_step, step[0])

            gb = [0]

            def load_gb(l, i):
                for dst, src in ((g_bc, ln_g), (b_bc, ln_b)):
                    pool.dma_start(dst[:, :], src[l, i:i + 1, :].to_broadcast([P, D])).then_inc(gb_in, 16)

            def load_layer(l):
                for par in range(2):
                    a = 64 * par
                    pool.dma_start(
                        wbd[a:a + 64, :, a:a + 64],
                        w_rg[l].rearrange("g (m q) i j -> q i (g m) j", q=2)[par]).then_inc(lay_in, 16)
                pool.dma_start(wif[:, :, :], w_in[l].rearrange("(k p) n -> p k n", p=P)[:, :, C_I:C_I + 8]).then_inc(lay_in, 16)
                pool.dma_start(bif[:, :], b_in[l:l + 1, C_I:C_I + 8].rearrange("o (g h) -> (o h) g", g=2),
                               allow_slow_non_contiguous=True).then_inc(lay_in, 16)
                pool.dma_start(cvb[:, :], b_in[l:l + 1, C_V:C_V + W].to_broadcast([P, W])).then_inc(lay_in, 16)
                pool.dma_start(bvb[:, :], b_in[l:l + 1, B_V:B_V + P].to_broadcast([P, P])).then_inc(lay_in, 16)
                pool.dma_start(snk[:, :], sinks[l:l + 1, :].to_broadcast([P, 8])).then_inc(lay_in, 16)

            nc.gpsimd.memset(xhi[:, :, 0:PAD].bitcast(F32), 0.0)
            nc.gpsimd.memset(xlo[:, :, 0:PAD].bitcast(F32), 0.0)
            nc.gpsimd.memset(half[:, :], -0.5)
            nc.gpsimd.memset(ones_d[:, :], 1.0 / W)
            link(nc.gpsimd.memset(wbd[:, :, :], 0.0))
            pool.dma_start(xtok[:, :, :], x[0].rearrange("(t p) d -> p t d", p=P)).then_inc(x_in, 16)
            for l in range(DEPTH):
                prow = S[:, 3 * l:3 * l + 3, 0:P]

                def row(tile, a, n, src):
                    pool.dma_start(prow[a:a + n, tile, :], src.rearrange("(r c) -> r c", c=P)).then_inc(rows_in[l], 16)

                row(0, PC_IN, 30, b_in[l, 0:C_I])
                row(0, PC_IN + 30, 40, b_in[l, D_A:N_IN])
                for h in range(2):
                    for u in range(2):
                        pool.dma_start(prow[PC_K2 + h:PC_K2 + h + 1, 0, 64 * u:64 * u + 64],
                                       b_in[l:l + 1, B_K + 64 * h:B_K + 64 * h + 64]).then_inc(rows_in[l], 16)
                row(0, PC_CW, 16, conv_w[l].rearrange("k c -> (k c)"))
                row(0, PC_CB, 4, conv_b[l])
                row(0, PC_RG, 8, b_rg[l].rearrange("g c -> (g c)"))
                row(0, PC_LAM, 4, lru_lambda[l])
                row(0, PC_DB, 4, dw_b[l])
                row(0, PC_CG, 4, cln_g[l])
                row(0, PC_CLB, 4, cln_b[l])
                row(1, 0, TAPS * KW, dw_w[l].rearrange("k c -> (k c)"))
                row(2, 0, 32, ln_g[l].rearrange("n c -> (n c)"))
                row(2, 32, 32, ln_b[l].rearrange("n c -> (n c)"))
            load_gb(0, 0)
            load_layer(0)
            for l in range(DEPTH):
                for i in range(4):
                    nn = 4 * l + i
                    for t in range(TT):
                        pool.wait_ge(var_made, 2 * nn + t + 1)
                        nc.gpsimd.tensor_tensor(rstd[:, t:t + 1], vare[:, t:t + 1], half[:, 0:1],
                                                ALU.pow).then_inc(rstd_made, 1)
                    pool.wait_ge(gb_in, 32 * (nn + 1))
                    for t in range(TT):
                        pool.wait_ge(xhat_made, 2 * nn + t + 1)
                        link(nc.gpsimd.tensor_tensor(xtok[:, t, :], r[:, t, :], g_bc[:, :], ALU.mult))
                        ins = nc.gpsimd.tensor_tensor(xtok[:, t, :], xtok[:, t, :], b_bc[:, :], ALU.add)
                        ins.then_inc(xtok_made, 1)
                    if nn < 4 * DEPTH - 1:
                        pool.wait_ge(xtok_made, 2 * (nn + 1))
                        load_gb((nn + 1) // 4, (nn + 1) % 4)
                    if i == 1:
                        if l + 1 < DEPTH:
                            load_layer(l + 1)
                        pool.dma_start(S[:, 3, 0:512].rearrange("p (t d) -> p t d", t=TT),
                                       p[l, 0].rearrange("(t p) d -> p t d", p=P)).then_inc(p_in, 16)
                        pool.dma_start(S[:, 4, :], ple_gate_b[l:l + 1, :].to_broadcast([P, D])).then_inc(pb_in, 16)
            pool.wait_ge(xtok_made, 8 * DEPTH)
            pool.dma_start(out[0].rearrange("(t p) d -> p t d", p=P), xtok[:, :, :]).then_inc(out_done, 16)
            pool.wait_ge(out_done, 16)


        @block.scalar
        def _(act):
            made = [0]
            step = [0]

            def link(ins):
                step[0] += 1
                ins.then_inc(act_step, 1)
                act.wait_ge(act_step, step[0])

            def hi(c, j=0, kv=False):
                slot = c % RING
                act.wait_ge(raw_full[slot], 32 * (c // RING + 1) + 32 * j)
                if c >= RING:
                    act.wait_ge(chunk_used, c - RING + 1 + RING * j)
                if kv:
                    src = raw[:, slot, 0:1024].rearrange("p (k n) -> p k n", k=4)
                    dst = whi[:, slot, 0:1536].rearrange("p (k n) -> p k n", k=4)
                    for h in range(2):
                        for u in range(2):
                            nc.scalar.copy(dst[:, :, 128 * h + 64 * u:128 * h + 64 * u + 64],
                                           src[:, :, 64 * h:64 * h + 64])
                    nc.scalar.copy(dst[:, :, 256:384], src[:, :, 128:256]).then_inc(whi_made, 1)
                else:
                    nc.scalar.copy(whi[:, slot, :], raw[:, slot, :]).then_inc(whi_made, 1)

            def his(upto, kv=()):
                while made[0] < min(upto, DEPTH * CHUNKS):
                    hi(made[0], kv=made[0] in kv)
                    made[0] += 1

            def ffn(c0, n0):
                def group(n, c, par, j=0):
                    act.wait_ge(gate0_done, n + 1)
                    nc.scalar.activation(sil[:, 0, :], ps[:, 0, 0:256], ACT.Silu).then_inc(silu_made, 1)
                    act.wait_ge(chunk_used, c + 1 + RING * j)
                    nc.scalar.activation(sil[:, 1, :], ps[:, 1, 0:256], ACT.Silu).then_inc(silu_made, 1)
                    act.wait_ge(h_made, 2 * n + 2)
                    nc.scalar.copy(hhi[:, par, :, :], hf[:, :, :]).then_inc(hhi_made, 1)

                his(c0 + 3)
                c = made[0]
                group(n0, c0 + 1, 0)
                with act.Fori(0, (NFF - 1) // 2) as j:
                    for u in range(2):
                        for k in range(3):
                            hi(c + 3 * u + k, 2 * j)
                        group(2 * j + (n0 + 1 + u), c0 + 3 + 3 * u, (1 + u) % 2, 2 * j)
                made[0] += FFN_CHUNKS - 3

            def split_x(n):
                for b in range(4):
                    act.wait_ge(xT_made, 4 * n + b + 1)
                    nc.scalar.copy(xhi[:, 2 * b:2 * b + 2, PAD:PAD + T], xT[:, 2 * b:2 * b + 2, :]).then_inc(xhi_made, 1)

            def evac(l, dst, func, col, bank, signal, tiles=KW):
                for m in range(tiles):
                    ins = nc.scalar.activation(dst[:, m, :], ps[:, bank + m // 2, 256 * (m % 2):256 * (m % 2) + 256],
                                               func, bias=pc[:, l, col + m:col + m + 1])
                ins.then_inc(signal, 1)

            def flat(bank, n):
                return ps[:, bank:bank + n, :].rearrange("p a b -> p (a b)")

            act.wait_ge(lam_abs, 1)
            nc.scalar.activation(spt[:, 1, :], spt[:, 0, :], ACT.Exp, scale=-1.0).then_inc(lam_exp, 1)
            his(2)
            split_x(0)
            for l in range(DEPTH):
                base = l * CHUNKS
                kv = (base + AT_STEP - 2, base + AT_STEP - 1)
                ffn(base + AT_FFN1, 2 * l * NFF)
                his(base + AT_IN + 2)
                split_x(4 * l + 1)

                def group(g):
                    his(base + AT_IN + 2 * g + 4, kv)
                    act.wait_ge(chunk_used, base + AT_IN + 2 * g + 2)

                group(0)
                evac(l, sg, ACT.Sigmoid, bias_col(D_G), 0, sgd_made)
                group(1)
                act.wait_ge(f_abs, l + 1)
                nc.scalar.activation(S[0:4, 7, 768:1024], S[0:4, 7, 512:768], ACT.Exp, scale=-1.0).then_inc(f_exp, 1)
                group(2)
                act.wait_ge(pads_made, l + 1)
                evac(l, axp[:, :, LTAPS - 1:], ACT.Identity, bias_col(A_X), 0, ax_made)
                group(3)
                evac(l, s4(2), ACT.Gelu_apprx_tanh, bias_col(A_Y), 2, gelu_made)
                group(4)
                act.wait_ge(rows_made, l + 1)
                evac(l, s4(6), ACT.Identity, bias_col(C_Q), 0, cq_made)
                act.wait_ge(rg_done, l + 1)
                evac(l, s4(3), ACT.Sigmoid, PC_RG, 4, gates_made)
                evac(l, s4(4), ACT.Sigmoid, PC_RG + 4, 6, gates_made)
                act.wait_ge(gates_made, 2 * l + 2)
                act.wait_ge(lam_made, 1)
                for m in range(KW):
                    nc.scalar.activation(s4(5)[:, m, :], s4(3)[:, m, :], ACT.Exp, scale=lam4[:, l, m:m + 1])
                for m in range(KW):
                    ins = nc.scalar.activation(s4(0)[:, m, :], s4(3)[:, m, :], ACT.Tanh, scale=lam4[:, l, m:m + 1])
                ins.then_inc(a_made, 1)
                group(5)
                evac(l, s4(7), ACT.Identity, bias_col(C_K), 2, ck_made)
                act.wait_ge(om_made, l + 1)
                nc.scalar.activation(S[:, 0, :], S[:, 3, :], ACT.Sqrt, scale=-1.0).then_inc(om_sqrt, 1)
                group(6)
                act.wait_ge(bA_made, l + 1)
                nc.scalar.copy(bhi[:, 0, :, :], s4(5)).then_inc(bhi_made, 1)
                act.wait_ge(e_arg, l + 1)
                nc.scalar.activation(Eflat, Eflat, ACT.Exp, scale=-1.0).then_inc(e_made, 1)
                nc.scalar.activation(emm[:, :, :], acol[:, 2:4, :], ACT.Exp, scale=-1.0).then_inc(emm_made, 1)
                group(7)
                evac(l, s4(1), ACT.Sigmoid, bias_col(C_O), 2, co_made)
                group(8)
                act.wait_ge(kq_done, l + 1)
                evac(l, qraw, ACT.Identity, bias_col(B_Q), 0, bq_made)
                group(9)
                evac(l, qraw[:, 4:6, :], ACT.Identity, PC_K2, 2, bk_made, tiles=2)
                for s in range(8):
                    n = ORDER[s // 2]
                    his(base + AT_STEP + 3 * s + 4)
                    if s == 0:
                        act.wait_ge(bC_made, l + 1)
                        nc.scalar.copy(bhi[:, 1, :, :], s4(1)).then_inc(bhi_made, 1)
                    act.wait_ge(chunk_used, base + AT_STEP + 3 * s + 2)
                    if s > 0:
                        act.wait_ge(prod_made, 8 * l + s)
                    evac(l, sg, ACT.Sigmoid, bias_col(GATES + n * D + (s % 2) * W), 0, sig_made)
                    if s == 1:
                        act.wait_ge(s_done, l + 1)
                        for pr in range(2):
                            ins = nc.scalar.activation(S[:, 6 + pr, :], flat(4 + 2 * pr, 2), ACT.Identity, scale=0.125)
                        ins.then_inc(s_out, 1)
                    if s == 2:
                        act.wait_ge(p_arg, l + 1)
                        nc.scalar.activation(soft[:, 3, :], soft[:, 2, :], ACT.Exp)
                        nc.scalar.activation(S[:, 6:8, :], S[:, 6:8, :], ACT.Exp).then_inc(p_exp, 1)
                        act.wait_ge(d_made, l + 1)
                        nc.scalar.activation(s4(1), yc, ACT.Square).then_inc(dsq_made, 1)
                    if s == 3:
                        act.wait_ge(dvar_made, l + 1)
                        nc.scalar.activation(S[:, 1, 0:256], S[:, 1, 0:256], ACT.Sqrt).then_inc(dstd_made, 1)
                        act.wait_ge(dn_made, l + 1)
                        for m in range(KW):
                            ins = nc.scalar.activation(s4(1)[:, m, :], yc[:, m, :], ACT.Silu,
                                                       scale=pc[:, l, PC_CG + m:PC_CG + m + 1],
                                                       bias=pc[:, l, PC_CLB + m:PC_CLB + m + 1])
                        ins.then_inc(bD_made, 1)
                    if s == 4:
                        act.wait_ge(bD_made, l + 1)
                        nc.scalar.copy(bhi[:, 1, :, :], s4(1)).then_inc(bhi_made, 1)
                        act.wait_ge(p_T, l + 1)
                        for pr in range(2):
                            ins = nc.scalar.copy(S[:, 4 + pr, :], flat(4 + 2 * pr, 2))
                        ins.then_inc(pt_made, 1)
                    if s == 5:
                        act.wait_ge(bB_made, l + 1)
                        nc.scalar.copy(bhi[:, 0, :, :], s4(2)).then_inc(bhi_made, 1)
                for h in range(2):
                    act.wait_ge(prod_made, 8 * l + 7 + h)
                    nc.scalar.copy(xhi[:, 4 * h:4 * h + 4, PAD:PAD + T], merged[:, 4 * h:4 * h + 4, :]).then_inc(mhi_made, 1)
                    his(base + AT_OUT + 2 + h)
                his(base + AT_FFN2 + 2)
                split_x(4 * l + 2)
                ffn(base + AT_FFN2, (2 * l + 1) * NFF)
                his(base + AT_PG + 2)
                split_x(4 * l + 3)
                act.wait_ge(pT_made, l + 1)
                nc.scalar.copy(phi, S[:, 3, 512:1024].rearrange("p (k t) -> p k t", k=2)).then_inc(phi_made, 1)
                his(base + AT_PW + 2)
                for t in range(TT):
                    act.wait_ge(z_made, 2 * l + t + 1)
                    nc.scalar.activation(S[:, 5 + t, :], S[:, 5 + t, :], ACT.Sigmoid).then_inc(zs_made, 1)
                his(base + CHUNKS + 2)
                if l + 1 < DEPTH:
                    split_x(4 * l + 4)

        @block.vector
        def _(dve):
            made = [0]
            step = [0]
            taps = [0]

            def link(ins):
                step[0] += 1
                ins.then_inc(vec_step, 1)
                dve.wait_ge(vec_step, step[0])

            def lo(c, j=0, kv=False):
                slot = c % RING
                dve.wait_ge(whi_made, c + 1 + RING * j)
                if kv:
                    src = raw[:, slot, 0:1024].rearrange("p (k n) -> p k n", k=4)
                    high = whi[:, slot, 0:1536].rearrange("p (k n) -> p k n", k=4)
                    dst = wlo[:, slot, 0:1536].rearrange("p (k n) -> p k n", k=4)
                    for a, b, w in [(0, 0, 64), (64, 0, 64), (128, 64, 64), (192, 64, 64), (256, 128, 128)]:
                        ins = nc.vector.tensor_tensor(dst[:, :, a:a + w], src[:, :, b:b + w],
                                                      high[:, :, a:a + w].bitcast(F32), ALU.subtract)
                    ins.then_inc(wlo_made, 1)
                else:
                    nc.vector.tensor_tensor(wlo[:, slot, :], raw[:, slot, :], whi[:, slot, :].bitcast(F32),
                                            ALU.subtract).then_inc(wlo_made, 1)

            def los(upto, kv=()):
                while made[0] < min(upto, DEPTH * CHUNKS):
                    lo(made[0], kv=made[0] in kv)
                    made[0] += 1

            def ffn(c0, n0):
                def group(n, par):
                    for q in range(2):
                        dve.wait_ge(silu_made, 2 * n + q + 1)
                        nc.vector.scalar_tensor_tensor(hf[:, q, :], sil[:, q, :], 0.5, ps[:, q, 256:512],
                                                       ALU.mult, ALU.mult).then_inc(h_made, 1)
                    dve.wait_ge(hhi_made, n + 1)
                    nc.vector.tensor_tensor(hlo[:, par, :, :], hf[:, :, :], hhi[:, par, :, :].bitcast(F32),
                                            ALU.subtract).then_inc(hlo_made, 1)

                los(c0 + 3)
                c = made[0]
                group(n0, 0)
                with dve.Fori(0, (NFF - 1) // 2) as j:
                    for u in range(2):
                        for k in range(3):
                            lo(c + 3 * u + k, 2 * j)
                        group(2 * j + (n0 + 1 + u), (1 + u) % 2)
                made[0] += FFN_CHUNKS - 3

            def make_xT(n, l=None, i=None):
                def low(b):
                    dve.wait_ge(xhi_made, 4 * n + b + 1)
                    nc.vector.tensor_tensor(xlo[:, 2 * b:2 * b + 2, PAD:PAD + T], xT[:, 2 * b:2 * b + 2, :],
                                            xhi[:, 2 * b:2 * b + 2, PAD:PAD + T].bitcast(F32),
                                            ALU.subtract).then_inc(xlo_made, 1)

                for b in range(4):
                    dve.wait_ge(xhat_T, 4 * n + b + 1)
                    for k in (2 * b, 2 * b + 1):
                        src = ps[:, b, 256 * (k % 2):256 * (k % 2) + 256]
                        if l is None:
                            ins = nc.vector.tensor_copy(xT[:, k, :], src)
                        else:
                            g = PC_G + 8 * i + k
                            ins = nc.vector.tensor_scalar(xT[:, k, :], src, pc[:, l, g:g + 1],
                                                          pc[:, l, g + 32:g + 33], ALU.mult, ALU.add)
                    ins.then_inc(xT_made, 1)
                    if b > 0:
                        low(b - 1)
                low(3)

            def norm(l, i, last_chunk, add=None):
                nn = 4 * l + i
                if nn == 0:
                    dve.wait_ge(x_in, 16)
                else:
                    dve.wait_ge(xtok_made, 2 * nn)
                for t in range(TT):
                    if t == 0:
                        dve.wait_ge(acc0_done, nn + 1)
                    else:
                        dve.wait_ge(chunk_used, last_chunk + 1)
                    acc = ps[:, 4 + 2 * t:6 + 2 * t, :].rearrange("p a b -> p (a b)")
                    if add is not None:
                        dve.wait_ge(zs_made, 2 * l + t + 1)
                        link(nc.vector.tensor_tensor(add[:, t, :], add[:, t, :], acc, ALU.mult))
                        acc = add[:, t, :]
                    link(nc.vector.scalar_tensor_tensor(r[:, t, :], xtok[:, t, :], ALPHA, acc, ALU.mult, ALU.add))
                    nc.vector.bn_stats(stats[:, t, 0, :], r[:, t, 0:512])
                    link(nc.vector.bn_stats(stats[:, t, 1, :], r[:, t, 512:1024]))
                    link(nc.vector.bn_aggr(mv[:, t, :], stats[:, t, :, :].rearrange("p a b -> p (a b)")))
                    nc.vector.tensor_scalar(vare[:, t:t + 1], mv[:, t, 1:2], EPS, None, ALU.add).then_inc(var_made, 1)
                    dve.wait_ge(rstd_made, 2 * nn + t + 1)
                    nc.vector.tensor_scalar(r[:, t, :], r[:, t, :], mv[:, t, 0:1], rstd[:, t:t + 1],
                                            ALU.subtract, ALU.mult).then_inc(xhat_made, 1)
                if nn < 4 * DEPTH - 1:
                    make_xT(nn + 1, l, i)

            def log1p(t, s, e, q, pl):
                link(nc.vector.tensor_scalar(s, e, 2.0, None, ALU.add))
                link(nc.vector.reciprocal(q, s))
                link(nc.vector.tensor_tensor(s, e, q, ALU.mult))
                link(nc.vector.tensor_tensor(q, s, s, ALU.mult))
                link(nc.vector.tensor_scalar(pl, q, 1.0 / 15, None, ALU.mult))
                for k in (13, 11, 9, 7, 5, 3):
                    link(nc.vector.scalar_tensor_tensor(pl, pl, 1.0 / k, q, ALU.add, ALU.mult))
                link(nc.vector.scalar_tensor_tensor(t, pl, 1.0, s, ALU.add, ALU.mult))

            def conv_taps(l, n):
                for _ in range(n):
                    k, m = divmod(taps[0] - l * TAPS * KW, KW)
                    if k >= TAPS:
                        return
                    w = pc[:, l, PC_DW + KW * k + m:PC_DW + KW * k + m + 1]
                    src = gl[:, m, k:k + T]
                    if k == 0:
                        ins = nc.vector.tensor_scalar(yc[:, m, :], src, w, pc[:, l, PC_DB + m:PC_DB + m + 1],
                                                      ALU.mult, ALU.add)
                    else:
                        dve.wait_ge(conv_tap, taps[0] - KW + 1)
                        ins = nc.vector.scalar_tensor_tensor(yc[:, m, :], src, w, yc[:, m, :], ALU.mult, ALU.add)
                    ins.then_inc(conv_tap, 1)
                    taps[0] += 1

            def branch_low(slot, src, count):
                dve.wait_ge(bhi_made, count)
                nc.vector.tensor_tensor(blo[:, slot, :, :], src, bhi[:, slot, :, :].bitcast(F32),
                                        ALU.subtract).then_inc(blo_made, 1)

            for l in range(DEPTH):
                dve.wait_ge(prow_T, l + 1)
                nc.vector.tensor_copy(pc[:, l, 0:ROWS0], ps[:, l, 0:ROWS0])
                nc.vector.tensor_copy(pc[:, l, ROWS0:PC_G], ps[:, l, P:P + TAPS * KW])
                link(nc.vector.tensor_copy(pc[:, l, PC_G:PCN], ps[:, l, 2 * P:2 * P + 64]))
            for l in range(DEPTH):
                lam = pc[:, l, PC_LAM:PC_LAM + 4]
                link(nc.vector.tensor_scalar(spt[:, 0, 4 * l:4 * l + 4], lam, -1.0, None, ALU.mult))
                link(nc.vector.tensor_scalar(spt[:, 5, 4 * l:4 * l + 4], spt[:, 0, 4 * l:4 * l + 4], 0.0, None, ALU.max))
                ins = nc.vector.tensor_tensor(spt[:, 0, 4 * l:4 * l + 4], spt[:, 0, 4 * l:4 * l + 4], lam, ALU.max)
                if l + 1 < DEPTH:
                    link(ins)
                else:
                    ins.then_inc(lam_abs, 1)
            los(2)
            make_xT(0)
            dve.wait_ge(lam_exp, 1)
            log1p(spt[:, 4, :], spt[:, 2, :], spt[:, 1, :], spt[:, 3, :], spt[:, 4, :])
            link(nc.vector.tensor_scalar(spt[:, 4, :], spt[:, 4, :], 2.0, None, ALU.mult))
            link(nc.vector.tensor_tensor(spt[:, 4, :], spt[:, 4, :], spt[:, 5, :], ALU.add))
            nc.vector.tensor_scalar(lam4[:, :, :].rearrange("p l m -> p (l m)"), spt[:, 4, :], -8.0, None,
                                    ALU.mult).then_inc(lam_made, 1)

            for l in range(DEPTH):
                base = l * CHUNKS
                kv = (base + AT_STEP - 2, base + AT_STEP - 1)
                ffn(base + AT_FFN1, 2 * l * NFF)
                los(base + AT_IN + 2)
                norm(l, 0, base + AT_IN - 1)

                def group(g):
                    los(base + AT_IN + 2 * g + 4, kv)
                    dve.wait_ge(chunk_used, base + AT_IN + 2 * g + 2)

                los(base + AT_IN + 4, kv)
                rw = [S[0:4, 7, 256 * k:256 * k + 256] for k in range(4)]
                rt = [S[0:4, 6, 256 * k:256 * k + 256] for k in range(4)]
                dve.wait_ge(lay_in, 112 * (l + 1))
                dve.wait_ge(if_done, l + 1)
                nc.vector.tensor_scalar(rw[0], ps[0:4, 4, 0:256], bif[:, 0:1], None, ALU.add)
                link(nc.vector.tensor_scalar(rw[1], ps[0:4, 4, 256:512], bif[:, 1:2], None, ALU.add))
                link(nc.vector.tensor_scalar(rt[0], rw[1], -1.0, None, ALU.mult))
                nc.vector.tensor_tensor(rw[2], rw[1], rt[0], ALU.max).then_inc(f_abs, 1)
                dve.wait_ge(xtok_made, 2 * (4 * l + 1))
                nc.vector.memset(gl[:, :, 0:TAPS - 1], 0.0)
                nc.vector.memset(axp[:, :, 0:LTAPS - 1], 0.0)
                nc.vector.memset(vext[:, :, :, P:P + 1], 1.0).then_inc(pads_made, 1)

                group(1)
                dve.wait_ge(sgd_made, l + 1)
                for m in range(KW):
                    ins = nc.vector.scalar_tensor_tensor(
                        gl[:, m, TAPS - 1:], ps[:, 2 + m // 2, 256 * (m % 2):256 * (m % 2) + 256],
                        pc[:, l, bias_col(D_A) + m:bias_col(D_A) + m + 1], sg[:, m, :], ALU.add, ALU.mult)
                ins.then_inc(glu_made, 1)
                dve.wait_ge(glu_made, l + 1)
                dve.wait_ge(pads_made, l + 1)
                conv_taps(l, 4)
                dve.wait_ge(f_exp, l + 1)
                log1p(rt[3], rt[0], rw[3], rt[1], rt[2])
                link(nc.vector.tensor_scalar(rw[1], rw[1], 0.0, None, ALU.min))
                link(nc.vector.scalar_tensor_tensor(rw[1], rt[3], -2.0, rw[1], ALU.mult, ALU.add))
                link(nc.vector.tensor_tensor_scan(rt[0], kc[0:4, K_ONE:K_ONE + T], rw[1], 0.0, ALU.mult, ALU.add))
                link(nc.vector.tensor_tensor(rows[:, 0, :], rw[0], rt[0], ALU.subtract))
                link(nc.vector.tensor_tensor_scan(rows[:, 1, :], rows[:, 0, :], rows[:, 0, :], 0.0, ALU.max, ALU.max))
                nc.vector.tensor_tensor(rows[:, 2, :], rows[:, 1, :], rt[0], ALU.add).then_inc(rows_made, 1)

                group(2)
                conv_taps(l, 4)
                dve.wait_ge(ax_made, l + 1)
                u = s4(1)
                for k in range(LTAPS):
                    for m in range(KW):
                        w = pc[:, l, PC_CW + KW * k + m:PC_CW + KW * k + m + 1]
                        if k == 0:
                            ins = nc.vector.tensor_scalar(u[:, m, :], axp[:, m, 0:T], w,
                                                          pc[:, l, PC_CB + m:PC_CB + m + 1], ALU.mult, ALU.add)
                        else:
                            ins = nc.vector.scalar_tensor_tensor(u[:, m, :], axp[:, m, k:k + T], w, u[:, m, :],
                                                                 ALU.mult, ALU.add)
                        if m < KW - 1 or k == LTAPS - 1:
                            if k == LTAPS - 1 and m == KW - 1:
                                ins.then_inc(u_made, 1)
                        else:
                            link(ins)
                group(3)
                conv_taps(l, 12)
                group(4)
                conv_taps(l, 12)
                group(5)
                dve.wait_ge(a_made, l + 1)
                dve.wait_ge(u_made, l + 1)
                link(nc.vector.tensor_tensor(S[:, 4, :], S[:, 4, :], S[:, 1, :], ALU.mult))
                link(nc.vector.tensor_tensor(S[:, 3, :], S[:, 5, :], S[:, 5, :], ALU.mult))
                nc.vector.scalar_tensor_tensor(S[:, 3, :], S[:, 3, :], 1.0, S[:, 0, :], ALU.add,
                                               ALU.mult).then_inc(om_made, 1)
                conv_taps(l, 6)
                group(6)
                for t in range(TT):
                    ins = nc.vector.tensor_tensor(
                        vext[:, t, :, 0:P], ps[:, t, :].rearrange("p (h e) -> p h e", h=4),
                        cvb[:, :].rearrange("p (h e) -> p h e", h=4), ALU.add)
                ins.then_inc(cv_made, 1)
                dve.wait_ge(om_sqrt, l + 1)
                link(nc.vector.tensor_tensor(S[:, 4, :], S[:, 4, :], S[:, 0, :], ALU.mult))
                for m in range(KW):
                    ins = nc.vector.tensor_tensor_scan(s4(3)[:, m, :], s4(5)[:, m, :], s4(4)[:, m, :], 0.0,
                                                       ALU.mult, ALU.add)
                link(ins)
                nc.vector.tensor_tensor(S[:, 5, :], S[:, 3, :], S[:, 2, :], ALU.mult).then_inc(bA_made, 1)
                dve.wait_ge(rows_T, l + 1)
                dve.wait_ge(bA_made, l + 1)
                link(nc.vector.tensor_copy(acol[:, :, :].rearrange("p a b -> p (a b)"), ps[:, 7, 0:16]))
                for h in range(4):
                    mt = ps[:, 5 + h // 2, 256 * (h % 2):256 * (h % 2) + 256]
                    nc.vector.tensor_scalar(E[:, h, 0:256], mt, acol[:, 0, h:h + 1], 0.0, ALU.subtract, ALU.max)
                    ins = nc.vector.tensor_scalar(E[:, h, 256:384], mt[:, P:T], acol[:, 1, h:h + 1], 0.0,
                                                  ALU.subtract, ALU.max)
                ins.then_inc(e_arg, 1)
                branch_low(0, s4(5), NB * l + 1)
                group(7)
                dve.wait_ge(kq_done, l + 1)
                dve.wait_ge(e_made, l + 1)
                dve.wait_ge(blo_made, NB * l + 1)
                for b in range(2):
                    nc.vector.scalar_tensor_tensor(scT[:, 2 * b:2 * b + 2, 0:256],
                                                   ps[:, 4 + b, :].rearrange("p (h t) -> p h t", h=2), P ** -0.5,
                                                   E[:, 2 * b:2 * b + 2, 0:256], ALU.mult, ALU.mult)
                link(nc.vector.scalar_tensor_tensor(scT[:, :, 256:384],
                                                    ps[:, 6, :].rearrange("p (h t) -> p h t", h=4), P ** -0.5,
                                                    E[:, :, 256:384], ALU.mult, ALU.mult))
                tri = kc[:, K_TRI:K_TRI + P].unsqueeze(1).to_broadcast([P, 4, P])
                nc.vector.tensor_tensor(scT[:, :, 0:P], scT[:, :, 0:P], tri, ALU.mult)
                nc.vector.tensor_tensor(scT[:, :, 256:384], scT[:, :, 256:384], tri, ALU.mult).then_inc(sc_made, 1)
                conv_taps(l, 8)
                group(8)
                conv_taps(l, 14)
                group(9)
                nc.vector.tensor_tensor(vw[:, :, :], ps[:, 3, :].rearrange("p (c e) -> p c e", c=NCH),
                                        bvb[:, :].unsqueeze(1).to_broadcast([P, NCH, P]), ALU.add).then_inc(vw_made, 1)
                dve.wait_ge(num_done, l + 1)
                dve.wait_ge(emm_made, l + 1)
                dcol = ps[:, 4:8, :].rearrange("p a (b e) -> p a b e", b=2)[:, :, :, P:P + 1]
                d4 = [den[:, k, :].rearrange("p (a b e) -> p a b e", a=4, b=2) for k in range(3)]
                link(nc.vector.tensor_scalar(d4[0], dcol, -1.0, None, ALU.mult))
                link(nc.vector.tensor_tensor(d4[0], dcol, d4[0], ALU.max))
                link(nc.vector.tensor_tensor(den[:, 1, :], den[:, 0, :], emm[:, :, :].rearrange("p a b -> p (a b)"), ALU.max))
                link(nc.vector.reciprocal(den[:, 2, :], den[:, 1, :]))
                nc.vector.tensor_tensor(
                    S[:, 0, :].rearrange("p (a b e) -> p a b e", a=4, b=2),
                    ps[:, 4:8, :].rearrange("p a (b e) -> p a b e", b=2)[:, :, :, 0:P],
                    d4[2].to_broadcast([P, 4, 2, P]), ALU.mult).then_inc(hc_made, 1)
                conv_taps(l, 10)
                for s in range(8):
                    los(base + AT_STEP + 3 * s + 4)
                    if s == 0:
                        dve.wait_ge(hc_T, l + 1)
                        dve.wait_ge(co_made, l + 1)
                        nc.vector.tensor_tensor(S[:, 1, :], ps[:, 4:6, :].rearrange("p a b -> p (a b)"), S[:, 1, :],
                                                ALU.mult).then_inc(bC_made, 1)
                        conv_taps(l, 3)
                        branch_low(1, s4(1), NB * l + 2)
                        dve.wait_ge(rot_done, l + 1)
                        cos = kc[:, K_COS:K_COS + T].unsqueeze(1)
                        sin = kc[:, K_SIN:K_SIN + T].unsqueeze(1)
                        nc.vector.tensor_tensor(qrot, ps[:, 4:7, :].rearrange("p a (b t) -> p (a b) t", b=2),
                                                sin.to_broadcast([P, 6, T]), ALU.mult)
                        nc.vector.memset(kr[:, :, 0:PAD], 0.0)
                        link(nc.vector.tensor_tensor(qraw, qraw, cos.to_broadcast([P, 6, T]), ALU.mult))
                        nc.vector.tensor_tensor(qr, qraw[:, 0:4, :], qrot[:, 0:4, :], ALU.add)
                        nc.vector.tensor_tensor(kr[:, :, PAD:], qraw[:, 4:6, :], qrot[:, 4:6, :], ALU.add).then_inc(rope_made, 1)
                        conv_taps(l, 10)
                    if s == 1:
                        conv_taps(l, TAPS * KW)
                    if s == 2:
                        dve.wait_ge(s_out, l + 1)
                        link(nc.vector.memset(Pm[0:L, 0, :, 0:L], MASKED))
                        link(nc.vector.tensor_reduce(soft[:, 0, :], S[:, 6:8, :].rearrange("p a (h j) -> p (a h) j", h=8),
                                                     AX_X, ALU.max))
                        sk = snk[:, :].rearrange("p (j u) -> p u j", u=2).unsqueeze(1).to_broadcast([P, 2, 2, 4])
                        v2 = [soft[:, k, :].rearrange("p (a u j) -> p a u j", a=2, u=2) for k in range(5)]
                        link(nc.vector.tensor_tensor(v2[1], v2[0], sk, ALU.max))
                        nc.vector.tensor_tensor(v2[2], sk, v2[1], ALU.subtract)
                        pf = S[:, 6:8, :].rearrange("p a (h j) -> p (a h) j", h=8)
                        nc.vector.tensor_tensor(pf, pf, soft[:, 1, :].unsqueeze(2).to_broadcast([P, 16, P]),
                                                ALU.subtract).then_inc(p_arg, 1)
                        dve.wait_ge(mean_done, l + 1)
                        dve.wait_ge(conv_tap, TAPS * KW * (l + 1))
                        nc.vector.tensor_tensor(yc, yc, ps[:, 4, 0:256].unsqueeze(1).to_broadcast([P, KW, T]),
                                                ALU.subtract).then_inc(d_made, 1)
                    if s == 3:
                        dve.wait_ge(dvar_done, l + 1)
                        nc.vector.tensor_scalar(S[:, 1, 0:256], ps[:, 5, 0:256], EPS, None, ALU.add).then_inc(dvar_made, 1)
                        dve.wait_ge(p_exp, l + 1)
                        link(nc.vector.tensor_reduce(soft[:, 0, :], pf, AX_X, ALU.add))
                        link(nc.vector.tensor_tensor(soft[:, 0, :], soft[:, 0, :], soft[:, 3, :], ALU.add))
                        link(nc.vector.reciprocal(soft[:, 4, :], soft[:, 0, :]))
                        nc.vector.tensor_tensor(pf, pf, soft[:, 4, :].unsqueeze(2).to_broadcast([P, 16, P]),
                                                ALU.mult).then_inc(p_made, 1)
                        dve.wait_ge(dstd_made, l + 1)
                        dve.wait_ge(d_made, l + 1)
                        link(nc.vector.reciprocal(S[:, 1, 256:512], S[:, 1, 0:256]))
                        nc.vector.tensor_tensor(yc, yc, S[:, 1, 256:512].unsqueeze(1).to_broadcast([P, KW, T]),
                                                ALU.mult).then_inc(dn_made, 1)
                    if s == 4:
                        branch_low(1, s4(1), NB * l + 3)
                    if s == 5:
                        dve.wait_ge(pv_done, l + 1)
                        nc.vector.tensor_copy(S[:, 2, :], ps[:, 4:6, :].rearrange("p a b -> p (a b)")).then_inc(bB_made, 1)
                        branch_low(0, s4(2), NB * l + 4)
                    los(base + AT_STEP + 3 * s + 5)
                    dve.wait_ge(chunk_used, base + AT_STEP + 3 * s + 3)
                    dve.wait_ge(sig_made, 8 * l + s + 1)
                    half_m = merged[:, 4 * (s % 2):4 * (s % 2) + 4, :].rearrange("p k t -> p (k t)")
                    br = ps[:, 2:4, :].rearrange("p a b -> p (a b)")
                    if s < 2:
                        nc.vector.tensor_tensor(half_m, br, S[:, 0, :], ALU.mult).then_inc(prod_made, 1)
                    else:
                        dve.wait_ge(prod_made, 8 * l + s)
                        link(nc.vector.tensor_tensor(S[:, 3, :], br, S[:, 0, :], ALU.mult))
                        nc.vector.tensor_tensor(half_m, half_m, S[:, 3, :], ALU.add).then_inc(prod_made, 1)
                    if s == 7:
                        for h in range(2):
                            dve.wait_ge(mhi_made, 2 * l + h + 1)
                            nc.vector.tensor_tensor(xlo[:, 4 * h:4 * h + 4, PAD:PAD + T], merged[:, 4 * h:4 * h + 4, :],
                                                    xhi[:, 4 * h:4 * h + 4, PAD:PAD + T].bitcast(F32),
                                                    ALU.subtract).then_inc(mlo_made, 1)
                            los(base + AT_OUT + 2 + h)
                los(base + AT_FFN2 + 2)
                norm(l, 1, base + AT_FFN2 - 1)
                ffn(base + AT_FFN2, (2 * l + 1) * NFF)
                los(base + AT_PG + 2)
                norm(l, 2, base + AT_PG - 1)
                pT = S[:, 3, 512:1024]
                dve.wait_ge(p_turned, l + 1)
                nc.vector.tensor_copy(pT, ps[:, 4, :]).then_inc(pT_made, 1)
                dve.wait_ge(phi_made, l + 1)
                nc.vector.tensor_tensor(plo, pT.rearrange("p (k t) -> p k t", k=2), phi.bitcast(F32),
                                        ALU.subtract).then_inc(plo_made, 1)
                los(base + AT_PW + 2)
                dve.wait_ge(pb_in, 16 * (l + 1))
                for t in range(TT):
                    if t == 0:
                        dve.wait_ge(pg0_done, l + 1)
                    else:
                        dve.wait_ge(chunk_used, base + AT_PW)
                    nc.vector.tensor_tensor(S[:, 5 + t, :], ps[:, 2 * t:2 * t + 2, :].rearrange("p a b -> p (a b)"),
                                            S[:, 4, :], ALU.add).then_inc(z_made, 1)
                los(base + CHUNKS + 2)
                norm(l, 3, base + AT_PW, add=S[:, 5:7, :])

        @block.tensor
        def _(pe):
            def mm3(dst, a_hi, a_lo, b_hi, b_lo, start, stop):
                nc.tensor.matmul(dst, a_hi, b_hi, start=start, stop=False, skip_group_check=True)
                nc.tensor.matmul(dst, a_hi, b_lo, start=False, stop=False, skip_group_check=True)
                return nc.tensor.matmul(dst, a_lo, b_hi, start=False, stop=stop, skip_group_check=True)

            def weights(c, k, n):
                slot = c % RING
                v = [w[:, slot, 0:k * n].rearrange("p (k n) -> p k n", k=k) for w in (whi, wlo)]
                return v

            def chunk_ready(c, j=0):
                pe.wait_ge(wlo_made, c + 1 + RING * j)

            def x_ready(n, k):
                pe.wait_ge(xlo_made, 4 * n + k // 2 + 1)

            def cm_chunk(c, kk, bank, bh, bl, first=True, last=True, waits=None):
                chunk_ready(c)
                w, v = weights(c, 4, W)
                for m in range(KW):
                    for k in range(4):
                        if waits is not None and m == 0 and k % 2 == 0:
                            x_ready(waits, 4 * kk + k)
                        ins = mm3(ps[:, bank + m // 2, 256 * (m % 2):256 * (m % 2) + 256],
                                  w[:, k, P * m:P * m + P], v[:, k, P * m:P * m + P],
                                  bh[:, 4 * kk + k, :], bl[:, 4 * kk + k, :],
                                  start=first and k == 0 and m % 2 == 0, stop=last and k == 3)
                ins.then_inc(chunk_used, 1)

            xh, xl = xhi[:, :, PAD:PAD + T], xlo[:, :, PAD:PAD + T]

            def tm_chunk(c, kk, kn, bank, cgs, ah, al, first, last, signal=None):
                w, v = weights(c, kn, W * len(cgs))
                for t in range(TT):
                    for i, cg in enumerate(cgs):
                        for k in range(kn):
                            ins = mm3(ps[:, bank + 2 * t + cg, :],
                                      ah(kk + k)[:, P * t:P * t + P], al(kk + k)[:, P * t:P * t + P],
                                      w[:, k, W * i:W * i + W], v[:, k, W * i:W * i + W],
                                      start=first and k == 0, stop=last and k == kn - 1)
                    if t == 0 and signal is not None:
                        ins.then_inc(signal, 1)
                ins.then_inc(chunk_used, 1)

            def tm_one(c, kk, bank, cg, signal=None):
                chunk_ready(c)
                w, v = weights(c, 4, W)
                for t in range(TT):
                    for k in range(4):
                        ins = mm3(ps[:, bank + 2 * t + cg, :], xh[:, 4 * kk + k, P * t:P * t + P],
                                  xl[:, 4 * kk + k, P * t:P * t + P], w[:, k, :], v[:, k, :],
                                  start=kk == 0 and k == 0, stop=kk == 1 and k == 3)
                    if t == 0 and signal is not None:
                        ins.then_inc(signal, 1)
                ins.then_inc(chunk_used, 1)

            def ffn(c0, n0, version, last_signal):
                def gate_up(n, c, j=0, fresh=False):
                    for kk in range(2):
                        chunk_ready(c + kk, j)
                        w, v = [a[:, (c + kk) % RING, :].rearrange("p (k u n) -> p k u n", k=4, u=2) for a in (whi, wlo)]
                        for q in range(2):
                            if kk == 0 and not (isinstance(n, int) and n == 0):
                                pe.wait_ge(h_made, 2 * n + q - 1)
                            for u in range(2):
                                for k in range(4):
                                    if fresh and q == 0 and u == 0 and k % 2 == 0:
                                        x_ready(version, 4 * kk + k)
                                    ins = mm3(ps[:, q, 256 * u:256 * u + 256],
                                              w[:, k, u, P * q:P * q + P], v[:, k, u, P * q:P * q + P],
                                              xh[:, 4 * kk + k, :], xl[:, 4 * kk + k, :],
                                              start=kk == 0 and u == 0 and k == 0, stop=kk == 1 and k == 3)
                            if kk == 1 and q == 0:
                                ins.then_inc(gate0_done, 1)
                        ins.then_inc(chunk_used, 1)

                def down(n, c, par, first, last, j=0, signal=None):
                    pe.wait_ge(hlo_made, n + 1)
                    chunk_ready(c, j)
                    tm_chunk(c, 0, 2, 4, (0, 1), lambda k: hhi[:, par, k, :], lambda k: hlo[:, par, k, :],
                             first, last, signal)

                gate_up(n0, c0, fresh=True)
                gate_up(n0 + 1, c0 + 2)
                down(n0, c0 + 4, 0, True, False)
                with pe.Fori(0, (NFF - 3) // 2) as j:
                    for u in range(2):
                        gate_up(2 * j + (n0 + 2 + u), c0 + 5 + 3 * u, 2 * j)
                        down(2 * j + (n0 + 1 + u), c0 + 7 + 3 * u, (1 + u) % 2, False, False, 2 * j)
                gate_up(n0 + NFF - 1, c0 + 3 * (NFF - 1) - 1)
                down(n0 + NFF - 2, c0 + 3 * (NFF - 1) + 1, (NFF - 2) % 2, False, False)
                down(n0 + NFF - 1, c0 + FFN_CHUNKS - 1, (NFF - 1) % 2, False, True, signal=last_signal)

            def turn_x(n, src):
                for t in range(TT):
                    if n > 0:
                        pe.wait_ge(xhat_made, 2 * (n - 1) + t + 1)
                    for k in range(KD):
                        ins = nc.tensor.transpose(ps[:, k // 2, 256 * (k % 2) + P * t:256 * (k % 2) + P * t + P],
                                                  src[:, t, P * k:P * k + P], ident)
                        if t == 1 and k % 2 == 1:
                            ins.then_inc(xhat_T, 1)

            pe.wait_ge(consts_in, 16)
            for l in range(DEPTH):
                prow = S[:, 3 * l:3 * l + 3, 0:P]
                pe.wait_ge(rows_in[l], 256)
                nc.tensor.transpose(ps[:, l, 0:ROWS0], prow[0:ROWS0, 0, :], ident[0:ROWS0, 0:ROWS0])
                nc.tensor.transpose(ps[:, l, P:P + TAPS * KW], prow[0:TAPS * KW, 1, :], ident[0:TAPS * KW, 0:TAPS * KW])
                nc.tensor.transpose(ps[:, l, 2 * P:2 * P + 64], prow[0:64, 2, :], ident[0:64, 0:64]).then_inc(prow_T, 1)
            pe.wait_ge(x_in, 16)
            pe.wait_ge(lam_abs, 1)
            turn_x(0, xtok)
            for l in range(DEPTH):
                base = l * CHUNKS
                nn = 4 * l
                ffn(base + AT_FFN1, 2 * l * NFF, nn, acc0_done)
                turn_x(nn + 1, r)

                out_by = [None, None, (sgd_made, l + 1), (glu_made, l + 1), (ax_made, l + 1), (gelu_made, l + 1),
                          (cq_made, l + 1), (ck_made, l + 1), (cv_made, l + 1), (co_made, l + 1)]

                def group(g):
                    off = GROUPS[g]
                    bank = 2 * (g % 2)
                    if out_by[g] is not None:
                        pe.wait_ge(*out_by[g])
                    for kk in range(2):
                        c = base + AT_IN + 2 * g + kk
                        if off == C_V:
                            chunk_ready(c)
                            w, v = weights(c, 4, W)
                            for t in range(TT):
                                for k in range(4):
                                    ins = mm3(ps[:, bank + t, :], xh[:, 4 * kk + k, P * t:P * t + P],
                                              xl[:, 4 * kk + k, P * t:P * t + P], w[:, k, :], v[:, k, :],
                                              start=kk == 0 and k == 0, stop=kk == 1 and k == 3)
                            ins.then_inc(chunk_used, 1)
                        elif off == "kv":
                            chunk_ready(c)
                            w, v = weights(c, 4, 384)
                            for m in range(2):
                                for k in range(4):
                                    mm3(ps[:, bank, 256 * m:256 * m + 256], w[:, k, P * m:P * m + P],
                                        v[:, k, P * m:P * m + P], xh[:, 4 * kk + k, :], xl[:, 4 * kk + k, :],
                                        start=kk == 0 and m == 0 and k == 0, stop=kk == 1 and k == 3)
                            for ch in range(NCH):
                                for k in range(4):
                                    ins = mm3(ps[:, bank + 1, P * ch:P * ch + P],
                                              xhi[:, 4 * kk + k, L * ch:L * ch + P], xlo[:, 4 * kk + k, L * ch:L * ch + P],
                                              w[:, k, 256:384], v[:, k, 256:384],
                                              start=kk == 0 and ch == 0 and k == 0, stop=kk == 1 and k == 3)
                            ins.then_inc(chunk_used, 1)
                        else:
                            cm_chunk(c, kk, bank, xh, xl, first=kk == 0, last=kk == 1,
                                     waits=nn + 1 if g == 0 else None)

                def mm(dst, a, b, start=True, stop=True):
                    return nc.tensor.matmul(dst, a, b, start=start, stop=stop, skip_group_check=True)

                group(0)
                pe.wait_ge(lay_in, 112 * (l + 1))
                for g in range(2):
                    for k in range(KD):
                        ins = mm(ps[0:4, 4, 256 * g:256 * g + 256], wif[:, k, 4 * g:4 * g + 4], xT[:, k, :],
                                 start=k == 0, stop=k == KD - 1)
                ins.then_inc(if_done, 1)
                group(1)
                group(2)
                group(3)
                pe.wait_ge(u_made, l + 1)
                for g in range(2):
                    for m in range(KW):
                        ins = mm(ps[:, 4 + 2 * g + m // 2, 256 * (m % 2):256 * (m % 2) + 256], wbd[:, KW * g + m, :],
                                 s4(1)[:, m, :])
                ins.then_inc(rg_done, 1)
                group(4)
                group(5)
                pe.wait_ge(rows_made, l + 1)
                pe.wait_ge(gates_made, 2 * l + 2)
                for t in range(TT):
                    nc.tensor.transpose(ps[:, 7, 4 * t:4 * t + 4], rows[:, 0, P * t:P * t + P], ident[0:4, 0:4])
                    nc.tensor.transpose(ps[:, 7, 8 + 4 * t:12 + 4 * t], rows[:, 2, P * t:P * t + P], ident[0:4, 0:4])
                for h in range(4):
                    ins = mm(ps[:, 5 + h // 2, 256 * (h % 2):256 * (h % 2) + 256], kc[0:4, K_SEL + P * h:K_SEL + P * h + P],
                             rows[:, 1, :])
                ins.then_inc(rows_T, 1)
                group(6)
                pe.wait_ge(e_arg, l + 1)
                pe.wait_ge(ck_made, l + 1)
                for h in range(4):
                    q, k = s4(6)[:, h, :], s4(7)[:, h, :]
                    mm(ps[:, 4 + h // 2, 256 * (h % 2):256 * (h % 2) + 256], k[:, 0:P], q)
                    ins = mm(ps[:, 6, P * h:P * h + P], k[:, P:T], q[:, P:T])
                ins.then_inc(kq_done, 1)
                group(7)
                group(8)
                pe.wait_ge(sc_made, l + 1)
                pe.wait_ge(cv_made, l + 1)
                for t in range(TT):
                    for h in range(4):
                        dst = ps[:, 4 + 2 * t + h // 2, 256 * (h % 2):256 * (h % 2) + P + 1]
                        ins = mm(dst, scT[:, h, P * t:P * t + P], vext[:, 0, h, :], stop=t == 0)
                        if t == 1:
                            ins = mm(dst, scT[:, h, 256:384], vext[:, 1, h, :], start=False)
                ins.then_inc(num_done, 1)
                group(9)
                pe.wait_ge(hc_made, l + 1)
                for h in range(4):
                    for t in range(TT):
                        a = 4 * t + h
                        ins = nc.tensor.transpose(ps[:, 4 + h // 2, 256 * (h % 2) + P * t:256 * (h % 2) + P * t + P],
                                                  S[:, 0, P * a:P * a + P], ident)
                ins.then_inc(hc_T, 1)
                for s in range(8):
                    n = ORDER[s // 2]
                    if s > 0:
                        pe.wait_ge(sig_made, 8 * l + s)
                    else:
                        pe.wait_ge(bq_made, l + 1)
                    for kk in range(2):
                        cm_chunk(base + AT_STEP + 3 * s + kk, kk, 0, xh, xl, first=kk == 0, last=kk == 1)
                    if s == 0:
                        pe.wait_ge(bC_made, l + 1)
                        pe.wait_ge(bk_made, l + 1)
                        for m in range(6):
                            ins = mm(ps[:, 4 + m // 2, 256 * (m % 2):256 * (m % 2) + 256], kc[:, K_ROT:K_ROT + P], qraw[:, m, :])
                        ins.then_inc(rot_done, 1)
                    if s == 1:
                        pe.wait_ge(rope_made, l + 1)
                        for ch in range(NCH):
                            for h in range(8):
                                a = 64 * (h % 2)
                                b = 64 * (ch % 2)
                                ins = mm(ps[b:b + 64, 4 + 2 * (ch // 2) + h % 2, P * (h // 2):P * (h // 2) + P],
                                         qr[a:a + 64, h // 2, L * ch:L * ch + L], kr[a:a + 64, h // 4, L * ch:L * ch + P])
                        ins.then_inc(s_done, 1)
                    if s == 2:
                        pe.wait_ge(conv_tap, TAPS * KW * (l + 1))
                        pe.wait_ge(s_out, l + 1)
                        for m in range(KW):
                            ins = mm(ps[:, 4, 0:256], ones_d[:, :], yc[:, m, :], start=m == 0, stop=m == KW - 1)
                        ins.then_inc(mean_done, 1)
                    if s == 3:
                        pe.wait_ge(dsq_made, l + 1)
                        for m in range(KW):
                            ins = mm(ps[:, 5, 0:256], ones_d[:, :], s4(1)[:, m, :], start=m == 0, stop=m == KW - 1)
                        ins.then_inc(dvar_done, 1)
                    if s == 4:
                        pe.wait_ge(p_made, l + 1)
                        pe.wait_ge(dvar_made, l + 1)
                        for pr in range(2):
                            for h in range(8):
                                ins = nc.tensor.transpose(ps[:, 4 + 2 * pr + h // 4, P * (h % 4):P * (h % 4) + P],
                                                          Pm[:, pr, h, :], ident)
                        ins.then_inc(p_T, 1)
                    if s == 5:
                        pe.wait_ge(pt_made, l + 1)
                        pe.wait_ge(vw_made, l + 1)
                        for ch in range(NCH):
                            for kv in range(2):
                                for par in range(2):
                                    dst = ps[64 * par:64 * par + 64, 4 + kv, :].rearrange("p (a t) -> p a t", a=2)
                                    b = 64 * (ch % 2)
                                    ins = mm(dst[:, :, L * ch:L * ch + L], vw[:, ch, 64 * kv:64 * kv + 64],
                                             PT[:, ch // 2, 4 * par + 2 * kv:4 * par + 2 * kv + 2, b:b + 64])
                        ins.then_inc(pv_done, 1)
                    pe.wait_ge(blo_made, NB * l + s // 2 + 1)
                    if s == 0:
                        pe.wait_ge(vw_made, l + 1)
                    else:
                        pe.wait_ge(prod_made, 8 * l + s)
                    slot = (0, 1, 1, 0)[s // 2]
                    cm_chunk(base + AT_STEP + 3 * s + 2, 0, 2, bhi[:, slot, :, :], blo[:, slot, :, :])
                for cg in range(2):
                    for kk in range(2):
                        c = base + AT_OUT + 2 * cg + kk
                        pe.wait_ge(mlo_made, 2 * l + kk + 1)
                        tm_one(c, kk, 4, cg, acc0_done if cg == 1 and kk == 1 else None)
                turn_x(nn + 2, r)
                ffn(base + AT_FFN2, (2 * l + 1) * NFF, nn + 2, acc0_done)
                turn_x(nn + 3, r)
                pe.wait_ge(p_in, 16 * (l + 1))
                for k in range(2):
                    for t in range(TT):
                        ins = nc.tensor.transpose(ps[:, 4, 256 * k + P * t:256 * k + P * t + P],
                                                  S[:, 3, 256 * t + P * k:256 * t + P * k + P], ident)
                ins.then_inc(p_turned, 1)
                x_ready(nn + 3, 6)
                for cg in range(2):
                    for kk in range(2):
                        c = base + AT_PG + 2 * cg + kk
                        tm_one(c, kk, 0, cg, pg0_done if cg == 1 and kk == 1 else None)
                pe.wait_ge(plo_made, l + 1)
                chunk_ready(base + AT_PW)
                tm_chunk(base + AT_PW, 0, 2, 4, (0, 1), lambda k: phi[:, k, :], lambda k: plo[:, k, :], True, True,
                         acc0_done)
                if l + 1 < DEPTH:
                    turn_x(nn + 4, r)


_INS = ["x", "p", "ln_g", "ln_b", "ffn_w_in", "ffn_w_out", "w_in", "b_in", "conv_w", "conv_b", "w_rg",
        "b_rg", "lru_lambda", "sinks", "dw_w", "dw_b", "cln_g", "cln_b", "w_br", "w_out", "ple_w",
        "ple_gate_w", "ple_gate_b"]


def kernel(**inputs):
    import concourse.bacc as bacc
    from concourse.bass_utils import run_bass_kernel_spmd

    nc = bacc.Bacc("TRN2", target_bir_lowering=False, num_devices=1)
    arrays = {f"in_{n}": np.ascontiguousarray(inputs[n]) for n in _INS}
    arrays["in_consts"] = constants()
    args = [nc.dram_tensor(n, a.shape, mybir.dt.from_np(a.dtype), kind="ExternalInput").ap()
            for n, a in arrays.items()]
    out = nc.dram_tensor("out_x", (1, T, D), F32, kind="ExternalOutput").ap()
    build(nc, *args, out)
    got = run_bass_kernel_spmd(nc, [arrays], core_ids=[0])
    return got.results[0]["out_x"]
```
